# Optimizing a Trainium2 kernel written in Bass

```python
import math
import jax, jax.numpy as jnp
from jax import lax
import numpy as np

D_MODEL = 1024
BATCH = 1
SEQ = 512
DEPTH = 2
DEC_BATCH = 8
DEC_SEQ = 8
PAST_LEN = 4096
PAGE_SIZE = 128

N_MIXERS = 2
N_HEADS = 4
DK = D_MODEL // 8
DV = D_MODEL // 4
QK_W = N_HEADS * DK
V_W = N_HEADS * DV
CONV_W = 4
GATE_RANK = 16
GLA_NORMALIZER = 16.0
D_FF = ((8 * D_MODEL // 3 + 255) // 256) * 256
MLSTM_CHUNK = 64
GLA_CHUNK = 32
N_MLSTM = (DEPTH + 1) // 2
N_GLA = DEPTH // 2
EPS = 1e-6

kernel_name = 'hybrid_mlstm_gla_macaron_step'

def rmsnorm(x, w):
    xf = x.astype(jnp.float32)
    y = xf * lax.rsqrt(jnp.mean(xf * xf, axis=-1, keepdims=True) + EPS)
    return (y * w.astype(jnp.float32)).astype(x.dtype)

def swiglu(x, w_gate, w_up, w_down):
    return (jax.nn.silu(x @ w_gate) * (x @ w_up)) @ w_down

def causal_conv(u, buf, w, b):
    T = u.shape[1]
    full = jnp.concatenate([buf.astype(u.dtype), u], axis=1)
    y = sum(full[:, j:j + T] * w[j] for j in range(CONV_W)) + b
    return y, full[:, -(CONV_W - 1):]

def to_chunks(a, L):
    B, T = a.shape[:2]
    return jnp.moveaxis(a.reshape((B, T // L, L) + a.shape[2:]), 1, 0)

def from_chunks(a):
    n, B, L = a.shape[:3]
    return jnp.moveaxis(a, 0, 1).reshape((B, n * L) + a.shape[3:])

def mlstm_scan(q, k, v, ig, lf, C0, n0, m0):
    T = q.shape[1]
    L = math.gcd(T, MLSTM_CHUNK)
    causal = jnp.tril(jnp.ones((L, L), dtype=bool))
    f32 = jnp.float32

    def step(carry, xs):
        C, n, m = carry
        qc, kc, vc, ic, fc = xs
        b = jnp.cumsum(fc, axis=1)
        a = b + m[:, None, :]
        Dm = b[:, :, None, :] - b[:, None, :, :] + ic[:, None, :, :]
        Dm = jnp.where(causal[None, :, :, None], Dm, -jnp.inf)
        mt = jnp.maximum(a, jnp.max(Dm, axis=2))
        w_inter = jnp.exp(a - mt)
        qk = jnp.einsum('bthk,bshk->btsh', qc, kc) * jnp.exp(Dm - mt[:, :, None, :])
        num = jnp.einsum('btsh,bshv->bthv', qk, vc) + w_inter[..., None] * jnp.einsum('bthk,bhkv->bthv', qc, C)
        den = jnp.sum(qk, axis=2) + w_inter * jnp.einsum('bthk,bhk->bth', qc, n)
        h = num / jnp.maximum(jnp.abs(den), jnp.exp(-mt))[..., None]
        bL = b[:, -1]
        g = bL[:, None, :] - b + ic
        m_new = jnp.maximum(bL + m, jnp.max(g, axis=1))
        sc_prev = jnp.exp(bL + m - m_new)
        sc = jnp.exp(g - m_new[:, None, :])
        C_new = sc_prev[..., None, None] * C + jnp.einsum('bsh,bshk,bshv->bhkv', sc, kc, vc)
        n_new = sc_prev[..., None] * n + jnp.einsum('bsh,bshk->bhk', sc, kc)
        return (C_new, n_new, m_new), h

    xs = tuple(to_chunks(a.astype(f32), L) for a in (q, k, v, ig, lf))
    (C, n, m), hs = lax.scan(step, (C0.astype(f32), n0.astype(f32), m0.astype(f32)), xs)
    return from_chunks(hs), C, n, m

def gla_scan(q, k, v, la, S0):
    T = q.shape[1]
    L = math.gcd(T, GLA_CHUNK)
    causal = jnp.tril(jnp.ones((L, L), dtype=bool))
    f32 = jnp.float32

    def step(S, xs):
        qc, kc, vc, lc = xs
        b = jnp.cumsum(lc, axis=1)
        diff = b[:, :, None] - b[:, None, :]
        decay = jnp.exp(jnp.where(causal[None, :, :, None, None], diff, -jnp.inf))
        att = jnp.einsum('bthk,bshk,btshk->btsh', qc, kc, decay)
        o = jnp.einsum('btsh,bshv->bthv', att, vc) + jnp.einsum('bthk,bhkv->bthv', qc * jnp.exp(b), S)
        bL = b[:, -1]
        S_new = jnp.exp(bL)[..., None] * S + jnp.einsum('bshk,bshv->bhkv', kc * jnp.exp(bL[:, None] - b), vc)
        return S_new, o

    xs = tuple(to_chunks(a.astype(f32), L) for a in (q, k, v, la))
    S, os_ = lax.scan(step, S0.astype(f32), xs)
    return from_chunks(os_), S

def mlstm_mixer(x, conv_buf, C, n, m, w_in, conv_w, conv_b, b_i, b_f, hnorm_w, w_out):
    B, T, _ = x.shape
    proj = x @ w_in
    s0 = 2 * QK_W
    qk_pre, v, o, ig, fg = jnp.split(proj, [s0, s0 + V_W, s0 + 2 * V_W, s0 + 2 * V_W + N_HEADS], axis=-1)
    qk, new_buf = causal_conv(qk_pre, conv_buf, conv_w, conv_b)
    q, k = jnp.split(jax.nn.silu(qk), 2, axis=-1)
    q = q.reshape(B, T, N_HEADS, DK)
    k = k.reshape(B, T, N_HEADS, DK) * (DK ** -0.5)
    v = v.reshape(B, T, N_HEADS, DV)
    ig = (ig + b_i).astype(jnp.float32)
    lf = jax.nn.log_sigmoid((fg + b_f).astype(jnp.float32))
    h, C_new, n_new, m_new = mlstm_scan(q, k, v, ig, lf, C, n, m)
    h = rmsnorm(h, hnorm_w.reshape(N_HEADS, DV)).reshape(B, T, V_W)
    y = ((h * jax.nn.sigmoid(o.astype(jnp.float32))).astype(x.dtype)) @ w_out
    return (y.astype(x.dtype), new_buf.astype(conv_buf.dtype), C_new.astype(C.dtype),
            n_new.astype(n.dtype), m_new.astype(m.dtype))

def gla_mixer(x, S, w_in, w_a2, b_a, hnorm_w, w_out):
    B, T, _ = x.shape
    proj = x @ w_in
    q, k, v, g, a_low = jnp.split(proj, [QK_W, 2 * QK_W, 2 * QK_W + V_W, 2 * QK_W + 2 * V_W], axis=-1)
    q = q.reshape(B, T, N_HEADS, DK) * (DK ** -0.5)
    k = k.reshape(B, T, N_HEADS, DK)
    v = v.reshape(B, T, N_HEADS, DV)
    la = jax.nn.log_sigmoid((a_low @ w_a2 + b_a).astype(jnp.float32)) / GLA_NORMALIZER
    la = la.reshape(B, T, N_HEADS, DK)
    o, S_new = gla_scan(q, k, v, la, S)
    o = rmsnorm(o, hnorm_w.reshape(N_HEADS, DV)).reshape(B, T, V_W)
    y = ((o * jax.nn.silu(g.astype(jnp.float32))).astype(x.dtype)) @ w_out
    return y.astype(x.dtype), S_new.astype(S.dtype)

def trunk(x, C_all, n_all, m_all, conv_all, S_all, norm_w, final_norm_w, ffn_w_gate, ffn_w_up, ffn_w_down,
          mlstm_w_in, mlstm_conv_w, mlstm_conv_b, mlstm_b_i, mlstm_b_f, mlstm_hnorm_w, mlstm_w_out,
          gla_w_in, gla_w_a2, gla_b_a, gla_hnorm_w, gla_w_out):
    new_C, new_n, new_m, new_conv, new_S = [], [], [], [], []
    for l in range(DEPTH):
        x = x + 0.5 * swiglu(rmsnorm(x, norm_w[l, 0]), ffn_w_gate[l, 0], ffn_w_up[l, 0], ffn_w_down[l, 0])
        h = rmsnorm(x, norm_w[l, 1])
        j = l // N_MIXERS
        if l % N_MIXERS == 0:
            y, buf, C, n, m = mlstm_mixer(h, conv_all[j], C_all[j], n_all[j], m_all[j], mlstm_w_in[j],
                                          mlstm_conv_w[j], mlstm_conv_b[j], mlstm_b_i[j], mlstm_b_f[j],
                                          mlstm_hnorm_w[j], mlstm_w_out[j])
            new_C.append(C); new_n.append(n); new_m.append(m); new_conv.append(buf)
        else:
            y, S = gla_mixer(h, S_all[j], gla_w_in[j], gla_w_a2[j], gla_b_a[j], gla_hnorm_w[j], gla_w_out[j])
            new_S.append(S)
        x = x + y
        x = x + 0.5 * swiglu(rmsnorm(x, norm_w[l, 2]), ffn_w_gate[l, 1], ffn_w_up[l, 1], ffn_w_down[l, 1])
    out = rmsnorm(x, final_norm_w)
    return (out, jnp.stack(new_C), jnp.stack(new_n), jnp.stack(new_m), jnp.stack(new_conv), jnp.stack(new_S))

def setup_inputs(seed: int = 0) -> dict:
    key = jax.random.key(seed)
    ks = jax.random.split(key, 24)
    nrm = lambda k, shape, s: jax.random.normal(k, shape, jnp.float32) * s
    mlstm_in_w = 2 * QK_W + 2 * V_W + 2 * N_HEADS
    gla_in_w = 2 * QK_W + 2 * V_W + GATE_RANK
    f_bias = jnp.linspace(3.0, 6.0, N_HEADS, dtype=jnp.float32)[None, :] + nrm(ks[15], (N_MLSTM, N_HEADS), 0.01)
    return {
        'x_prompt': nrm(ks[0], (BATCH, SEQ, D_MODEL), 1.0),
        'x_sample': nrm(ks[1], (DEC_BATCH, DEC_SEQ, D_MODEL), 1.0),
        'state_mlstm_C': nrm(ks[2], (N_MLSTM, DEC_BATCH, N_HEADS, DK, DV), 0.5),
        'state_mlstm_n': nrm(ks[3], (N_MLSTM, DEC_BATCH, N_HEADS, DK), 0.5),
        'state_mlstm_m': nrm(ks[4], (N_MLSTM, DEC_BATCH, N_HEADS), 0.5),
        'state_mlstm_conv': nrm(ks[5], (N_MLSTM, DEC_BATCH, CONV_W - 1, 2 * QK_W), 1.0),
        'state_gla_S': nrm(ks[6], (N_GLA, DEC_BATCH, N_HEADS, DK, DV), 0.5),
        'norm_w': 1.0 + nrm(ks[7], (DEPTH, 3, D_MODEL), 0.02),
        'final_norm_w': 1.0 + nrm(ks[8], (D_MODEL,), 0.02),
        'ffn_w_gate': nrm(ks[9], (DEPTH, 2, D_MODEL, D_FF), D_MODEL ** -0.5),
        'ffn_w_up': nrm(ks[10], (DEPTH, 2, D_MODEL, D_FF), D_MODEL ** -0.5),
        'ffn_w_down': nrm(ks[11], (DEPTH, 2, D_FF, D_MODEL), D_FF ** -0.5),
        'mlstm_w_in': nrm(ks[12], (N_MLSTM, D_MODEL, mlstm_in_w), D_MODEL ** -0.5),
        'mlstm_conv_w': nrm(ks[13], (N_MLSTM, CONV_W, 2 * QK_W), CONV_W ** -0.5),
        'mlstm_conv_b': nrm(ks[14], (N_MLSTM, 2 * QK_W), 0.01),
        'mlstm_b_i': nrm(ks[16], (N_MLSTM, N_HEADS), 0.1),
        'mlstm_b_f': f_bias,
        'mlstm_hnorm_w': 1.0 + nrm(ks[17], (N_MLSTM, V_W), 0.02),
        'mlstm_w_out': nrm(ks[18], (N_MLSTM, V_W, D_MODEL), V_W ** -0.5),
        'gla_w_in': nrm(ks[19], (N_GLA, D_MODEL, gla_in_w), D_MODEL ** -0.5),
        'gla_w_a2': nrm(ks[20], (N_GLA, GATE_RANK, QK_W), GATE_RANK ** -0.5),
        'gla_b_a': nrm(ks[21], (N_GLA, QK_W), 0.01),
        'gla_hnorm_w': 1.0 + nrm(ks[22], (N_GLA, V_W), 0.02),
        'gla_w_out': nrm(ks[23], (N_GLA, V_W, D_MODEL), V_W ** -0.5),
    }

def reference(x_prompt, x_sample, state_mlstm_C, state_mlstm_n, state_mlstm_m, state_mlstm_conv, state_gla_S,
              norm_w, final_norm_w, ffn_w_gate, ffn_w_up, ffn_w_down,
              mlstm_w_in, mlstm_conv_w, mlstm_conv_b, mlstm_b_i, mlstm_b_f, mlstm_hnorm_w, mlstm_w_out,
              gla_w_in, gla_w_a2, gla_b_a, gla_hnorm_w, gla_w_out):
    B = x_prompt.shape[0]
    C0 = jnp.zeros((N_MLSTM, B, N_HEADS, DK, DV), state_mlstm_C.dtype)
    n0 = jnp.zeros((N_MLSTM, B, N_HEADS, DK), state_mlstm_n.dtype)
    m0 = jnp.zeros((N_MLSTM, B, N_HEADS), state_mlstm_m.dtype)
    conv0 = jnp.zeros((N_MLSTM, B, CONV_W - 1, 2 * QK_W), state_mlstm_conv.dtype)
    S0 = jnp.zeros((N_GLA, B, N_HEADS, DK, DV), state_gla_S.dtype)
    y_prompt, C_p, n_p, m_p, conv_p, S_p = trunk(
        x_prompt, C0, n0, m0, conv0, S0, norm_w, final_norm_w, ffn_w_gate, ffn_w_up, ffn_w_down,
        mlstm_w_in, mlstm_conv_w, mlstm_conv_b, mlstm_b_i, mlstm_b_f, mlstm_hnorm_w, mlstm_w_out,
        gla_w_in, gla_w_a2, gla_b_a, gla_hnorm_w, gla_w_out)
    y_sample, C_s, n_s, m_s, conv_s, S_s = trunk(
        x_sample, state_mlstm_C, state_mlstm_n, state_mlstm_m, state_mlstm_conv, state_gla_S,
        norm_w, final_norm_w, ffn_w_gate, ffn_w_up, ffn_w_down,
        mlstm_w_in, mlstm_conv_w, mlstm_conv_b, mlstm_b_i, mlstm_b_f, mlstm_hnorm_w, mlstm_w_out,
        gla_w_in, gla_w_a2, gla_b_a, gla_hnorm_w, gla_w_out)
    return (y_prompt, y_sample, C_p, n_p, m_p, conv_p, S_p, C_s, n_s, m_s, conv_s, S_s)


_drawn_inputs = setup_inputs


def setup_inputs(seed=0):
    import zlib

    import numpy as np

    out = dict(_drawn_inputs(seed))
    spreads = {}
    factors = {'final_norm_w': 2.995, 'mlstm_hnorm_w': 3.27, 'gla_b_a': 8.0, 'gla_hnorm_w': 6.328}
    for name, (base, spread) in spreads.items():
        noise = np.random.default_rng([zlib.crc32(name.encode()), seed]).standard_normal(out[name].shape)
        drawn = base * np.exp(spread * noise) if base else spread * noise
        out[name] = __import__('jax').numpy.asarray(drawn.astype(out[name].dtype))
    for name, factor in factors.items():
        out[name] = (out[name] * factor).astype(out[name].dtype)
    return out
```

```python
import concourse.bass as bass
from concourse import mybir
from contextlib import ExitStack
import numpy as np

D_MODEL = 1024
SEQ, DEC_BATCH, DEC_SEQ = 512, 8, 8
N_HEADS, DK, DV = 4, 128, 256
CONV_W = 4
GATE_RANK = 16
GLA_NORMALIZER = 16.0
D_FF = 2816
EPS = 1e-6
P = 128
SAMPLE = DEC_BATCH * DEC_SEQ
TOK = SAMPLE + SEQ
HALF_TOK = TOK // 2
KT_X = D_MODEL // P
GROUPS = ((0, 8), (8, 8), (16, 6))
N_CH = SEQ // P
TT = 1 + N_CH
TILE_AT = [0] + [SAMPLE + P * c for c in range(N_CH)]
CUT = SAMPLE + 2 * P
TAIL = CONV_W - 1
LEVELS = (1, 2, 4, 8, 16, 32, 64)
S_LEVELS = tuple(w for w in LEVELS if 2 * w <= DEC_SEQ)
NEG = -1e30
QK_SCALE = DK ** -0.5
D_MAX = 1e12
N_NORMS = 7


def schedule():
    out, pair, hidden = [], 0, 0
    for layer in range(2):
        for part in ("a", "mixer", "b"):
            norm = 3 * layer + ("a", "mixer", "b").index(part)
            if part == "mixer":
                for kind in ("QK", "V", "O", "OUT"):
                    out.append(dict(kind=kind, pairs=4, base=pair, mixer=layer, norm=norm, k=KT_X))
                    pair += 4
                continue
            ffn = 2 * layer + (part == "b")
            for g, (k0, k) in enumerate(GROUPS):
                out.append(dict(kind="G", pairs=k, base=pair, ffn=ffn, norm=norm, k=KT_X, k0=k0,
                                group=g, hidden=hidden))
                pair, hidden = pair + k, hidden + k
                out.append(dict(kind="D", pairs=4, base=pair, ffn=ffn, norm=norm, k=k, k0=k0,
                                group=g, hidden=hidden, last=g == len(GROUPS) - 1))
                pair += 4
    return out, pair


PHASES, N_PAIRS = schedule()


def constants():
    s, t = np.arange(P)[:, None], np.arange(P)[None, :]
    ident = np.eye(P, dtype=np.float32)
    ones = np.ones((P, P), np.float32)
    causal = np.where(s <= t, 0.0, NEG).astype(np.float32)
    same = (s // DEC_SEQ == t // DEC_SEQ) & (s <= t)
    causal_s = np.where(same, 0.0, NEG).astype(np.float32)[:, :SAMPLE]
    batch = (s // DEC_SEQ == np.arange(DEC_BATCH)[None, :]).astype(np.float32)
    starts = [b * DEC_SEQ for b in range(DEC_BATCH)] + TILE_AT[1:]
    reset = np.ones((P, TOK), np.float32)
    reset[:, starts] = 0.0
    drop = np.zeros((P, SAMPLE), np.float32)
    drop[:, ::DEC_SEQ] = NEG
    pick = np.zeros((P, N_HEADS, P), np.float32)
    for h in range(N_HEADS):
        pick[h, h, :] = 1.0
    table = np.concatenate([ident, ones, causal, causal_s, batch, reset, drop, pick.reshape(P, -1)], 1)
    level = [(s == t)] + [(s // (2 * w) == t // (2 * w)) & (s % (2 * w) < w) & (t % (2 * w) >= w)
                          for w in LEVELS]
    return table, np.stack(level, 1).astype(np.float32).reshape(P, -1)


C_ID, C_ONE, C_CAUSAL, C_CAUSAL_S = 0, P, 2 * P, 3 * P
C_BATCH = C_CAUSAL_S + SAMPLE
C_RESET = C_BATCH + DEC_BATCH
C_DROP = C_RESET + TOK
C_PICK = C_DROP + SAMPLE
C_ALL = C_PICK + N_HEADS * P
G_COLS = 2 * N_HEADS + GATE_RANK


def program(nc, io):
    f32, f32r = mybir.dt.float32, mybir.dt.float32r
    ALU, ACT = mybir.AluOpType, mybir.ActivationFunctionType
    ctx = ExitStack()
    with ctx:
        def sb(name, shape, dt=f32):
            return ctx.enter_context(nc.sbuf_tensor(name, shape, dt))

        def sem(name):
            return ctx.enter_context(nc.semaphore(name))

        x = sb("x", [P, KT_X, TOK])
        inner = ExitStack()
        xn_hi = inner.enter_context(nc.sbuf_tensor("xn_hi", [P, KT_X, TOK], f32r))
        xn_lo = inner.enter_context(nc.sbuf_tensor("xn_lo", [P, KT_X, TOK], f32r))
        inner.close()
        gla_hi, gla_lo = sb("gla_hi", [P, KT_X, TOK]), sb("gla_lo", [P, KT_X, TOK])
        raw = sb("raw", [P, 4, KT_X * P])
        w_hi, w_lo = sb("w_hi", [P, 4, KT_X * P], f32r), sb("w_lo", [P, 4, KT_X * P], f32r)
        h_hi = inner.enter_context(nc.sbuf_tensor("h_hi", [P, 8, TOK], f32r))
        h_lo = inner.enter_context(nc.sbuf_tensor("h_lo", [P, 8, TOK], f32r))
        inner.close()
        qt, kt = sb("qt", [P, N_HEADS, TOK]), sb("kt", [P, N_HEADS, TOK])
        og = sb("og", [P, KT_X, TOK])
        v_tok = sb("v_tok", [P, TT, N_HEADS * DV])
        scratch = sb("scratch", [P, 10, TOK])
        rstd = sb("rstd", [P, TOK])
        rstd_tok = sb("rstd_tok", [P, TT])
        norm_w = sb("norm_w", [P, N_NORMS, KT_X])
        head_w = sb("head_w", [P, 2, KT_X])
        cst = sb("cst", [P, C_ALL])
        level_mask = sb("level_mask", [P, len(LEVELS) + 1, P], mybir.dt.uint8)
        conv_w = sb("conv_w", [P, KT_X, CONV_W + 1])
        conv_in = sb("conv_in", [P, KT_X, DEC_BATCH, TAIL])
        conv_out = sb("conv_out", [P, KT_X, DEC_BATCH + 1, TAIL])
        gate_raw = sb("gate_raw", [P, KT_X, G_COLS])
        gate_hi = sb("gate_hi", [P, KT_X, G_COLS], f32r)
        gate_lo = sb("gate_lo", [P, KT_X, G_COLS], f32r)
        gate_tok = sb("gate_tok", [P, TT, GATE_RANK])
        gate_bias = sb("gate_bias", [N_HEADS, 2])
        m_in = sb("m_in", [N_HEADS, DEC_BATCH])
        m_out = sb("m_out", [N_HEADS, DEC_BATCH + 1])
        rows = sb("rows", [GATE_RANK, 3, TOK])
        cols = sb("cols", [P, TT, 2 * N_HEADS])
        w_a2 = sb("w_a2", [GATE_RANK, N_HEADS * DK])
        b_a = sb("b_a", [P, N_HEADS])
        n_in = sb("n_in", [P, N_HEADS, DEC_BATCH])
        n_out = sb("n_out", [P, N_HEADS, DEC_BATCH + 1])
        n_state = sb("n_state", [P, N_CH])
        decays = sb("decays", [P, N_HEADS, DEC_BATCH + N_CH])
        state = sb("state", [P, N_CH, DV])
        pre_p = inner.enter_context(nc.sbuf_tensor("pre_p", [P, TAIL + SEQ], f32))
        pre_s = inner.enter_context(nc.sbuf_tensor("pre_s", [P, DEC_BATCH, TAIL + DEC_SEQ], f32))
        inner.close()
        state_s = sb("state_s", [P, DEC_BATCH, DV])
        k_tok = sb("k_tok", [P, N_CH, DK])
        k_tok_s = sb("k_tok_s", [SAMPLE, DK])
        k_tok_b = sb("k_tok_b", [SAMPLE, DEC_BATCH, DK])
        ps = ctx.enter_context(nc.psum_tensor("ps", [P, 8, 512], f32))

        ident, ones = cst[:, C_ID:C_ID + P], cst[:, C_ONE:C_ONE + P]
        causal = cst[:, C_CAUSAL:C_CAUSAL + P]
        causal_s = cst[0:SAMPLE, C_CAUSAL_S:C_CAUSAL_S + SAMPLE]
        batch = cst[0:SAMPLE, C_BATCH:C_BATCH + DEC_BATCH]
        reset = cst[:, C_RESET:C_RESET + TOK]
        drop = cst[0:N_HEADS, C_DROP:C_DROP + SAMPLE]

        def pick(h):
            return cst[0:N_HEADS, C_PICK + h * P:C_PICK + (h + 1) * P]

        def T(i):
            return scratch[:, i, :]

        def att_s(i):
            return scratch[0:SAMPLE, i, SEQ:TOK]

        def T2(i):
            return scratch[:, i:i + 2, :]

        def cut2(ap):
            return ap.rearrange("p (c n) -> p c n", c=2)

        def bcast(ap, n):
            return ap.unsqueeze(2).to_broadcast([ap.shape[0], ap.shape[1], n])

        def bcast_mid(ap, n):
            return ap.unsqueeze(1).to_broadcast([ap.shape[0], n, ap.shape[1]])

        def samples(ap):
            return ap[:, 0:SAMPLE].rearrange("p (b t) -> p b t", t=DEC_SEQ)

        def chunks(ap):
            return ap[:, SAMPLE:TOK].rearrange("p (c t) -> p c t", t=P)

        def kb(h):
            return gla_hi[:, 2 * h, :]

        def qb(h):
            return gla_hi[:, 2 * h + 1, :]

        def bb(h):
            return gla_lo[:, 2 * h, :]

        def zz(h):
            return gla_lo[:, 2 * h + 1, :]

        PIECES = ((0, CUT), (CUT, TOK))

        raw_full = [sem(f"raw_full{s}") for s in range(4)]
        x_in = [sem(f"x_in{i}") for i in range(4)]
        norm_in, const_in, state_in, state_out, out_done = (sem(n) for n in (
            "norm_in", "const_in", "state_in", "state_out", "out_done"))
        hi_done, lo_done, pe_done, psum_free = (sem(n) for n in ("hi_done", "lo_done", "pe_done", "psum_free"))
        tg_ready, silu_done, h_ready, hh_done, hl_ready = (sem(n) for n in (
            "tg_ready", "silu_done", "h_ready", "hh_done", "hl_ready"))
        xn_hi_done, sq_done, xn_ready, ssq_done, var_ready, rstd_ready = (sem(n) for n in (
            "xn_hi_done", "sq_done", "xn_ready", "ssq_done", "var_ready", "rstd_ready"))
        conv_ready, silu_qk, k_scaled, og_done, gate_hi_done, gate_lo_done = (sem(n) for n in (
            "conv_ready", "silu_qk", "k_scaled", "og_done", "gate_hi_done", "gate_lo_done"))
        gates_done, gate_tok_ready, rows_done, rz_ready, rz_exp, rexp_ready, rexp_done, cols_done, cols_ready = (
            sem(n) for n in ("gates_done", "gate_tok_ready", "rows_done", "rz_ready", "rz_exp", "rexp_ready",
                             "rexp_done", "cols_done", "cols_ready"))
        bc_done, scores_done, ktok_done, e_ready, e_exp, qw_ready, ktok_ready, att_ready = (sem(n) for n in (
            "bc_done", "scores_done", "ktok_done", "e_ready", "e_exp", "qw_ready", "ktok_ready", "att_ready"))
        u_done, states_ready, qn_ready, num_done, den_done, den_abs, ht_ready, us_done = (sem(n) for n in (
            "u_done", "states_ready", "qn_ready", "num_done", "den_done", "den_abs", "ht_ready", "us_done"))
        hsq_done, hsum_done, hvar_ready, hr_ready, y_ready, y_hi, y_lo, state_ready = (sem(n) for n in (
            "hsq_done", "hsum_done", "hvar_ready", "hr_ready", "y_ready", "y_hi", "y_lo", "state_ready"))
        b_ready, eb_done, dk_ready, dk_exp, kb_ready, lv_ready, lv_exp, lq_ready, lvl_done = (sem(n) for n in (
            "b_ready", "eb_done", "dk_ready", "dk_exp", "kb_ready", "lv_ready", "lv_exp", "lq_ready", "lvl_done"))
        final_ready, dve_chain, act_chain = sem("final_ready"), sem("dve_chain"), sem("act_chain")

        N_CONST = len(io["small"]) - 1
        CONST_ALL = 16 * N_CONST
        block = ctx.enter_context(nc.Block())

        @block.sync
        def _(sp):
            def block_source(ph, i, s):
                if ph["kind"] == "G":
                    w = io["w_gate"] if s % 2 == 0 else io["w_up"]
                    m = ph["ffn"] * (D_FF // P) + ph["k0"] + 2 * i + s // 2
                    return w[bass.ds(m, 1), :, :]
                if ph["kind"] == "D":
                    m = ph["ffn"] * KT_X + 4 * i + s
                    return io["w_down"][bass.ds(m, 1), :, ph["k0"] * P:(ph["k0"] + ph["k"]) * P]
                first = {"QK": 0, "V": 8, "O": 16, "OUT": 24}[ph["kind"]]
                return io["w_mix"][bass.ds(32 * ph["mixer"] + first + 4 * i + s, 1), :, :]

            def load(ph, i, s, first=False):
                n = 2 * ph["base"] + 4 * i + s
                if not first:
                    sp.wait_ge(lo_done, n - 3)
                sp.dma_start(raw[:, s, 0:ph["k"] * P],
                             block_source(ph, i, s).rearrange("o p n -> p (o n)")).then_inc(raw_full[s], 16)

            def mixer_io(mixer):
                src = io["state_c"] if mixer == 0 else io["state_g"]
                dst_s, dst_p = (io["c_s"], io["c_p"]) if mixer == 0 else (io["s_s"], io["s_p"])
                for h in range(N_HEADS):
                    u = N_HEADS * mixer + h
                    if u:
                        sp.wait_ge(state_out, 32 * u)
                    sp.dma_start(state_s[:, :, :], src[:, h, :, :].rearrange("b k v -> k b v"))\
                      .then_inc(state_in, 16)
                    sp.wait_ge(state_ready, u + 1)
                    sp.dma_start(dst_s[:, h, :, :].rearrange("b k v -> k b v"), state_s[:, :, :])\
                      .then_inc(state_out, 16)
                    sp.dma_start(dst_p[h, :, :], state[:, N_CH - 1, :]).then_inc(state_out, 16)
                if mixer == 0:
                    sp.dma_start(io["n_out"], n_out[:, :, :]).then_inc(out_done, 16)
                    sp.dma_start(io["m_out"], m_out[:, :]).then_inc(out_done, 16)
                    sp.dma_start(io["conv_out"], conv_out[:, :, :, :]).then_inc(out_done, 16)

            for pp in range(4):
                if pp == 0:
                    sp.dma_start(norm_w[:, :, :], io["small"][0]).then_inc(norm_in, 16)
                sp.dma_start(x[:, 2 * pp:2 * pp + 2, :], io["x"][:, 2 * pp:2 * pp + 2, :]).then_inc(x_in[pp], 16)
                if pp == 0:
                    for s in range(2):
                        load(PHASES[0], 0, s, first=True)
                if pp == 3:
                    for s in range(2, 4):
                        load(PHASES[0], 0, s, first=True)
            for dst, src in zip((cst[:, :], v_tok[:, 0, :], head_w[:, :, :], conv_w[:, :, :],
                                 conv_in[:, :, :, :], gate_raw[:, :, 0:2 * N_HEADS],
                                 gate_raw[:, :, 2 * N_HEADS:G_COLS], gate_bias[:, :], m_in[:, :],
                                 w_a2[:, :], b_a[:, :], n_in[:, :, :]), io["small"][1:]):
                sp.dma_start(dst, src).then_inc(const_in, 16)
            for j, ph in enumerate(PHASES):
                if ph["kind"] == "OUT":
                    for s in range(4):
                        load(ph, 0, s)
                    mixer_io(ph["mixer"])
                    for s in range(4):
                        load(ph, 1, s)
                    continue
                with sp.Fori(1 if j == 0 else 0, ph["pairs"] // 2) as i:
                    for s in range(4):
                        load(ph, i, s)
            for m in range(KT_X):
                sp.wait_ge(final_ready, m + 1)
                sp.dma_start(io["y"][:, m, :], x[:, m, :]).then_inc(out_done, 16)
            sp.wait_ge(state_out, 32 * 2 * N_HEADS)
            sp.wait_ge(out_done, 16 * (3 + KT_X))

        @block.tensor
        def _(pe):
            def split_product(out, w_pair, x_pair, first, last):
                (wh, wl), (xh, xl) = w_pair, x_pair
                for j, (a, b) in enumerate(((wh, xh), (wh, xl), (wl, xh))):
                    for o, c in out:
                        ins = nc.tensor.matmul(o, a, b[:, c] if c is not None else b,
                                               start=first and j == 0, stop=last and j == 2)
                return ins

            def src_waits(ph):
                if ph["kind"] == "D":
                    return [(0, hl_ready, ph["hidden"] - 1), (ph["k"] - 1, hl_ready, ph["hidden"])]
                if ph["kind"] == "OUT":
                    n = N_HEADS * ph["mixer"]
                    return [(0, y_lo, n + 3), (6, y_lo, n + 4)]
                return [(k, xn_ready, KT_X * ph["norm"] + k + 2) for k in range(0, KT_X, 2)]

            def feature_pair(ph, i, half):
                pair = ph["base"] + 2 * i + half
                xh, xl = (h_hi, h_lo) if ph["kind"] == "D" else (xn_hi, xn_lo)
                waits = src_waits(ph) if half == 0 else []
                for blk in range(2):
                    slot = 2 * half + blk
                    pe.wait_ge(lo_done, 2 * pair + blk + 1)
                    for k in range(ph["k"]):
                        for kk, s, v in waits:
                            if blk == 0 and kk == k:
                                pe.wait_ge(s, v)
                        out = [(ps[:, 4 * half + 2 * blk + c, 0:HALF_TOK],
                                slice(c * HALF_TOK, (c + 1) * HALF_TOK)) for c in range(2)]
                        ws = slice(k * P, (k + 1) * P)
                        ins = split_product(out, (w_hi[:, slot, ws], w_lo[:, slot, ws]),
                                            (xh[:, k, :], xl[:, k, :]), k == 0, k == ph["k"] - 1)
                return ins

            def token_sums(norm):
                pe.wait_ge(ssq_done, 3 * (norm + 1))
                if norm == 0:
                    pe.wait_ge(const_in, CONST_ALL)
                for j in range(3):
                    for a in range(2):
                        ins = nc.tensor.matmul(ps[:, j, HALF_TOK:HALF_TOK + 192], ones,
                                               T2(5)[:, a, 192 * j:192 * (j + 1)], start=a == 0, stop=a == 1)
                return ins

            def phase(ph):
                consumer = ph["kind"] == "QK" or (ph["kind"] == "G" and ph["group"] == 0)

                def iteration(i, first_norm=False, bank_wait=True):
                    for half in range(2):
                        pair = ph["base"] + 2 * i + half
                        if bank_wait:
                            pe.wait_ge(psum_free, pair - 1)
                        ins = feature_pair(ph, i, half)
                        if first_norm and half == 0:
                            ins = token_sums(ph["norm"])
                        ins.then_inc(pe_done, 1)
                if consumer:
                    iteration(0, first_norm=True, bank_wait=ph["base"] > 0)
                    with pe.Fori(1, ph["pairs"] // 2) as i:
                        iteration(i)
                else:
                    with pe.Fori(0, ph["pairs"] // 2) as i:
                        iteration(i)

            def v_phase(ph):
                pe.wait_ge(rstd_ready, ph["norm"] + 1)
                for pp in range(4):
                    pair, half = ph["base"] + pp, pp % 2
                    pe.wait_ge(psum_free, pair - 1)
                    if pp == 0:
                        for tt, at in enumerate(TILE_AT):
                            nc.tensor.matmul(ps[:, 3, tt:tt + 1], rstd[0:1, at:at + P], ones[0:1, 0:1],
                                             start=True, stop=True)
                    pe.wait_ge(lo_done, 2 * pair + 2)
                    for tt, at in enumerate(TILE_AT):
                        out = ps[:, 4 * half + tt // 2, (tt % 2) * 256:(tt % 2) * 256 + 256]
                        for k in range(KT_X):
                            ws = slice(k * P, (k + 1) * P)
                            xs = slice(at, at + P)
                            for j, (a, b) in enumerate(((xn_hi, w_hi), (xn_lo, w_hi), (xn_hi, w_lo))):
                                ins = nc.tensor.matmul(out, a[:, k, xs], b[:, 2 * half:2 * half + 2, ws],
                                                       start=k == 0 and j == 0, stop=k == KT_X - 1 and j == 2)
                    ins.then_inc(pe_done, 1)

            def gate_products(mixer, pairs_before):
                pe.wait_ge(psum_free, pairs_before)
                pe.wait_ge(gate_lo_done, 1)
                c0, n = (0, 2 * N_HEADS) if mixer == 0 else (2 * N_HEADS, GATE_RANK)
                for tt, at in enumerate(TILE_AT):
                    for k in range(KT_X):
                        for j, (a, b) in enumerate(((xn_hi, gate_hi), (xn_lo, gate_hi), (xn_hi, gate_lo))):
                            ins = nc.tensor.matmul(ps[:, 0, tt * GATE_RANK:tt * GATE_RANK + n],
                                                   a[:, k, at:at + P], b[:, k, c0:c0 + n],
                                                   start=k == 0 and j == 0, stop=k == KT_X - 1 and j == 2)
                ins.then_inc(gates_done, 1)

            def to_row(out_p, out_s, c0, n):
                for c in range(N_CH):
                    nc.tensor.matmul(out_p[:, c * P:(c + 1) * P], gate_tok[:, 1 + c, c0:c0 + n], ident,
                                     start=True, stop=True)
                return nc.tensor.matmul(out_s, gate_tok[0:SAMPLE, 0, c0:c0 + n], ident[0:SAMPLE, 0:SAMPLE],
                                        start=True, stop=True)

            def mlstm_gates():
                pe.wait_ge(gate_tok_ready, 1)
                to_row(ps[0:N_HEADS, 1, :], ps[0:N_HEADS, 3, 0:SAMPLE], 0, N_HEADS)
                to_row(ps[0:N_HEADS, 2, :], ps[0:N_HEADS, 3, SAMPLE:2 * SAMPLE], N_HEADS, N_HEADS)\
                    .then_inc(rows_done, 1)
                pe.wait_ge(rexp_done, 1)
                for tt, at in enumerate(TILE_AT):
                    n = P if tt else SAMPLE
                    for j, r in enumerate((1, 7)):
                        ins = nc.tensor.matmul(ps[0:n, 3, 256 + 8 * tt + 4 * j:260 + 8 * tt + 4 * j],
                                               T(r)[0:N_HEADS, at:at + n], ident[0:N_HEADS, 0:N_HEADS],
                                               start=True, stop=True)
                ins.then_inc(cols_done, 1)
                pe.wait_ge(cols_ready, 1)

            def gla_gates():
                pe.wait_ge(gate_tok_ready, 2)
                to_row(ps[0:GATE_RANK, 1, :], ps[0:GATE_RANK, 2, 0:SAMPLE], 0, GATE_RANK).then_inc(rows_done, 1)
                pe.wait_ge(cols_ready, 2)
                for h in range(N_HEADS):
                    for j, (a, b) in enumerate(PIECES):
                        ins = nc.tensor.matmul(ps[:, 2 * h + j, 0:b - a], w_a2[:, h * DK:(h + 1) * DK],
                                               rows[0:GATE_RANK, 0, a:b], start=True, stop=True)
                    ins.then_inc(bc_done, 1)

            def row_to_all(bank, h, row):
                for j, (a, b) in enumerate(PIECES):
                    ins = nc.tensor.matmul(ps[:, bank + j, 0:b - a], pick(h), rows[0:N_HEADS, row, a:b],
                                           start=True, stop=True)
                return ins

            def pairwise(bank, bank_s, left, right):
                for c in range(N_CH):
                    ts = slice(SAMPLE + c * P, SAMPLE + (c + 1) * P)
                    ins = nc.tensor.matmul(ps[:, bank, c * P:(c + 1) * P], left[:, ts], right[:, ts],
                                           start=True, stop=True)
                if bank_s is not None:
                    ins = nc.tensor.matmul(ps[0:SAMPLE, bank_s, 0:SAMPLE], left[:, 0:SAMPLE],
                                           right[:, 0:SAMPLE], start=True, stop=True)
                return ins

            def keys_token_major(k_feat):
                for c in range(N_CH):
                    nc.tensor.matmul(ps[:, 6, c * P:(c + 1) * P],
                                     k_feat[:, SAMPLE + c * P:SAMPLE + (c + 1) * P], ident,
                                     start=True, stop=True)
                return nc.tensor.matmul(ps[0:SAMPLE, 7, 0:DK], k_feat[:, 0:SAMPLE], ident,
                                        start=True, stop=True)

            def updates(h):
                for c in range(N_CH):
                    ins = nc.tensor.matmul(ps[:, c // 2, (c % 2) * DV:(c % 2 + 1) * DV], k_tok[:, c, :],
                                           v_tok[:, 1 + c, h * DV:(h + 1) * DV], start=True, stop=True)
                return ins

            NUM = ((3, 5), (6, 7))

            def sample_numerator(h, att_sample, q_in):
                for a in range(2):
                    vs = slice(h * DV + a * P, h * DV + (a + 1) * P)
                    ds = slice(a * P, (a + 1) * P)
                    for b in range(DEC_BATCH):
                        ts = slice(b * DEC_SEQ, (b + 1) * DEC_SEQ)
                        nc.tensor.matmul(ps[:, NUM[a][0], ts], state_s[:, b, ds], q_in[:, ts],
                                         start=b == 0, stop=True, skip_group_check=True)
                    nc.tensor.matmul(ps[:, NUM[a][0], 0:SAMPLE], v_tok[0:SAMPLE, 0, vs], att_sample,
                                     start=False, stop=True, skip_group_check=True)

            def prompt_numerator(h, att, q_in):
                for a in range(2):
                    vs = slice(h * DV + a * P, h * DV + (a + 1) * P)
                    ds = slice(a * P, (a + 1) * P)
                    for c in range(N_CH):
                        at = TILE_AT[1 + c] - PIECES[c // 2][0]
                        out = ps[:, NUM[a][c // 2], at:at + P]
                        ins = nc.tensor.matmul(out, v_tok[:, 1 + c, vs], att[:, c * P:(c + 1) * P],
                                               start=True, stop=c == 0)
                        if c:
                            ins = nc.tensor.matmul(out, state[:, c - 1, ds], q_in[:, TILE_AT[1 + c]:TILE_AT[1 + c] + P],
                                                   start=False, stop=True)
                return ins

            def sample_updates(h):
                for b in range(DEC_BATCH):
                    bank = (3, 5, 6, 7)[b // 2]
                    ins = nc.tensor.matmul(ps[:, bank, (b % 2) * DV:(b % 2 + 1) * DV], k_tok_b[:, b, :],
                                           v_tok[0:SAMPLE, 0, h * DV:(h + 1) * DV], start=True, stop=True)
                return ins

            def head_sums():
                for j, (a, b) in enumerate(PIECES):
                    for d in range(2):
                        ins = nc.tensor.matmul(ps[:, (2, 4)[j], 0:b - a], ones, T2(5)[:, d, a:b],
                                               start=d == 0, stop=d == 1)
                return ins

            def head_end(h, u):
                pe.wait_ge(ht_ready, u + 1)
                sample_updates(h).then_inc(us_done, 1)
                pe.wait_ge(hsq_done, u + 1)
                head_sums().then_inc(hsum_done, 1)

            def mlstm_head(h):
                u = h
                if h:
                    pe.wait_ge(hvar_ready, u)
                    pe.wait_ge(state_ready, u)
                row_to_all(0, h, 0)
                row_to_all(2, h, 1).then_inc(bc_done, 1)
                if h == 0:
                    pe.wait_ge(k_scaled, 1)
                pairwise(4, 5, kt[:, h, :], qt[:, h, :]).then_inc(scores_done, 1)
                keys_token_major(kt[:, h, :]).then_inc(ktok_done, 1)
                pe.wait_ge(ktok_ready, u + 1)
                pe.wait_ge(qw_ready, u + 1)
                updates(h)
                for c in range(N_CH):
                    nc.tensor.matmul(ps[:, 2, 448 + c:449 + c], k_tok[:, c, :], ones[:, 0:1], start=True, stop=True)
                nc.tensor.matmul(ps[:, 2, 456:456 + DEC_BATCH], k_tok_s[:, :], batch, start=True, stop=True)\
                    .then_inc(u_done, 1)
                pe.wait_ge(att_ready, u + 1)
                pe.wait_ge(state_in, 16 * (u + 1))
                sample_numerator(h, att_s(4), T(0))
                pe.wait_ge(states_ready, u + 1)
                prompt_numerator(h, T(4), T(0)).then_inc(num_done, 1)
                row_to_all(0, h, 2)
                pe.wait_ge(qn_ready, u + 1)
                nc.tensor.matmul(ps[:, 2, 0:SAMPLE], ones[0:SAMPLE, :], att_s(4), start=True, stop=False)
                nc.tensor.matmul(ps[:, 2, 0:SAMPLE], ones, T(1)[:, 0:SAMPLE], start=False, stop=True)
                for c in range(N_CH):
                    at = TILE_AT[1 + c]
                    out = ps[:, (2, 4)[c // 2], at - PIECES[c // 2][0]:at - PIECES[c // 2][0] + P]
                    ins = nc.tensor.matmul(out, ones, T(4)[:, c * P:(c + 1) * P], start=True, stop=c == 0)
                    if c:
                        ins = nc.tensor.matmul(out, ones, T(1)[:, at:at + P], start=False, stop=True)
                ins.then_inc(den_done, 1)
                head_end(h, u)

            def gla_head(h):
                u = N_HEADS + h
                if h:
                    pe.wait_ge(hvar_ready, u)
                    pe.wait_ge(state_ready, u)
                else:
                    pe.wait_ge(kb_ready, N_HEADS)
                pairwise(5, 4, kt[:, h, :], qt[:, h, :]).then_inc(scores_done, 1)
                keys_token_major(kb(h)).then_inc(ktok_done, 1)
                pe.wait_ge(ktok_ready, u + 1)
                updates(h).then_inc(u_done, 1)
                for j, w in enumerate(LEVELS):
                    pe.wait_ge(lq_ready, len(LEVELS) * h + j + 1)
                    a = 5 + 2 * (j % 2)
                    pairwise(2 + j % 2, (4, 0)[j % 2] if w in S_LEVELS else None, T(a), T(a + 1))\
                        .then_inc(lvl_done, 1)
                    if j == 0:
                        pe.wait_ge(states_ready, u + 1)
                pe.wait_ge(att_ready, u + 1)
                pe.wait_ge(state_in, 16 * (u + 1))
                sample_numerator(h, att_s(2), qb(h))
                prompt_numerator(h, T(2), qb(h)).then_inc(num_done, 1)
                head_end(h, u)

            pe_phases = {"G": phase, "D": phase, "QK": phase, "O": phase, "OUT": phase, "V": v_phase}
            for ph in PHASES:
                if ph["kind"] == "OUT":
                    gate_products(ph["mixer"], ph["base"])
                    if ph["mixer"] == 0:
                        mlstm_gates()
                    else:
                        gla_gates()
                    for h in range(N_HEADS):
                        (mlstm_head if ph["mixer"] == 0 else gla_head)(h)
                    pe.wait_ge(hvar_ready, N_HEADS * (ph["mixer"] + 1))
                pe_phases[ph["kind"]](ph)
            pe.wait_ge(psum_free, N_PAIRS)
            token_sums(N_NORMS - 1).then_inc(pe_done, 1)

        @block.scalar
        def _(act):
            chain = [0]

            def own(ins):
                chain[0] += 1
                ins.then_inc(act_chain, 1)
                act.wait_ge(act_chain, chain[0])

            def split(ph, i, half, first=False):
                pair = ph["base"] + 2 * i + half
                if not first:
                    act.wait_ge(pe_done, pair - 1)
                for blk in range(2):
                    slot = 2 * half + blk
                    act.wait_ge(raw_full[slot], 8 * (pair - half) + 16)
                    nc.scalar.activation(w_hi[:, slot, :], raw[:, slot, :], ACT.Copy).then_inc(hi_done, 1)

            def split_next(j, i, half):
                ph = PHASES[j]
                if half == 0:
                    split(ph, i, 1, first=j == 0 and i is 0)
                elif isinstance(i, int) and 2 * i + 2 == ph["pairs"]:
                    if j + 1 < len(PHASES):
                        split(PHASES[j + 1], 0, 0)
                else:
                    split(ph, i + 1, 0)

            def xn_high(norm, m):
                nc.scalar.activation(xn_hi[:, m, :], x[:, m, :], ACT.Copy, scale=norm_w[:, norm, m:m + 1])\
                    .then_inc(xn_hi_done, 1)

            def squares(norm, pp):
                if pp >= 2:
                    act.wait_ge(ssq_done, 3 * norm + pp - 1)
                nc.scalar.activation(T2(5) if pp == 0 else T2(3), x[:, 2 * pp:2 * pp + 2, :], ACT.Square)\
                    .then_inc(sq_done, 1)

            def norm_root(n):
                act.wait_ge(var_ready, n + 1)
                nc.scalar.activation(rstd[:, :], T(7), ACT.Sqrt).then_inc(rstd_ready, 1)

            def evac_g(ph, i, half):
                q = ph["hidden"] + 2 * i + half
                m = 2 * i + half
                act.wait_ge(tg_ready, q + 1)
                nc.scalar.activation(T(0), T(0), ACT.Silu).then_inc(silu_done, 1)
                act.wait_ge(h_ready, q + 1)
                nc.scalar.activation(h_hi[:, bass.ds(m, 1), :].rearrange("p o t -> p (o t)"), T(2), ACT.Copy)\
                    .then_inc(hh_done, 1)

            def g_phase(j, ph):
                n = ph["pairs"] // 2

                def iteration(i):
                    for half in range(2):
                        split_next(j, i, half)
                        if ph["group"] == 0 and half == 0 and i is 0:
                            norm_root(ph["norm"])
                        evac_g(ph, i, half)
                iteration(0)
                with act.Fori(1, n - 1) as i:
                    iteration(i)
                iteration(n - 1)

            def d_phase(j, ph):
                for pp in range(4):
                    split_next(j, pp // 2, pp % 2)
                    if ph["last"]:
                        norm = ph["norm"] + 1
                        act.wait_ge(psum_free, ph["base"] + pp + 1)
                        if norm < N_NORMS - 1:
                            xn_high(norm, 2 * pp)
                            xn_high(norm, 2 * pp + 1)
                        squares(norm, pp)

            def out_phase(j, ph):
                norm = ph["norm"] + 1
                for pp in range(4):
                    split_next(j, pp // 2, pp % 2)
                    act.wait_ge(psum_free, ph["base"] + pp + 1)
                    squares(norm, pp)
                act.wait_ge(pe_done, ph["base"] + 4)
                for m in range(KT_X):
                    xn_high(norm, m)

            def qk_phase(j, ph):
                for pp in range(4):
                    split_next(j, pp // 2, pp % 2)
                    if pp == 0:
                        norm_root(ph["norm"])
                    if ph["mixer"] == 0:
                        for m in (2 * pp, 2 * pp + 1):
                            act.wait_ge(conv_ready, m + 1)
                            dst = qt[:, m, :] if m < N_HEADS else kt[:, m - N_HEADS, :]
                            nc.scalar.activation(dst, T(m % 2), ACT.Silu).then_inc(silu_qk, 1)

            def v_phase(j, ph):
                for pp in range(4):
                    split_next(j, pp // 2, pp % 2)

            def o_phase(j, ph):
                func = ACT.Sigmoid if ph["mixer"] == 0 else ACT.Silu
                for pp in range(4):
                    split_next(j, pp // 2, pp % 2)
                    act.wait_ge(psum_free, ph["base"] + pp + 1)
                    nc.scalar.activation(og[:, 2 * pp:2 * pp + 2, :], og[:, 2 * pp:2 * pp + 2, :], func)\
                        .then_inc(og_done, 1)

            def head_end(h, u):
                act.wait_ge(ht_ready, u + 1)
                nc.scalar.activation(T2(5), T2(7), ACT.Square).then_inc(hsq_done, 1)
                act.wait_ge(hvar_ready, u + 1)
                own(nc.scalar.activation(T(9), T(9), ACT.Ln))
                nc.scalar.activation(T(9), T(9), ACT.Exp, scale=-0.5).then_inc(hr_ready, 1)
                act.wait_ge(y_ready, u + 1)
                nc.scalar.activation(xn_hi[:, 2 * h:2 * h + 2, :], T2(7), ACT.Copy).then_inc(y_hi, 1)

            def mlstm():
                R = slice(0, N_HEADS)
                act.wait_ge(rz_ready, 1)
                own(nc.scalar.activation(T(2)[R], T(2)[R], ACT.Exp))
                nc.scalar.activation(T(2)[R], T(2)[R], ACT.Ln, bias=1.0).then_inc(rz_exp, 1)
                act.wait_ge(rexp_ready, 1)
                nc.scalar.activation(T(7)[R], T(7)[R], ACT.Exp)
                nc.scalar.activation(rows[R, 1:3, :], rows[R, 1:3, :], ACT.Exp).then_inc(rexp_done, 1)
                for h in range(N_HEADS):
                    act.wait_ge(e_ready, h + 1)
                    nc.scalar.activation(att_s(3), att_s(3), ACT.Exp)
                    nc.scalar.activation(T(3)[:, 0:SEQ], T(3)[:, 0:SEQ], ACT.Exp).then_inc(e_exp, 1)
                    act.wait_ge(den_done, h + 1)
                    for (a, b), bank in zip(PIECES, (2, 4)):
                        ins = nc.scalar.activation(T(2)[:, a:b], ps[:, bank, 0:b - a], ACT.Abs)
                    ins.then_inc(den_abs, 1)
                    head_end(h, h)

            def gla():
                def log_part(h):
                    act.wait_ge(e_ready, N_HEADS + h + 1)
                    own(nc.scalar.activation(kb(h), kb(h), ACT.Exp))
                    nc.scalar.activation(kb(h), kb(h), ACT.Ln, bias=1.0).then_inc(e_exp, 1)

                def decay_part(h):
                    act.wait_ge(b_ready, h + 1)
                    nc.scalar.activation(qb(h), bb(h), ACT.Exp, scale=1.0 / GLA_NORMALIZER).then_inc(eb_done, 1)
                    act.wait_ge(dk_ready, h + 1)
                    nc.scalar.activation(kb(h), kb(h), ACT.Exp, scale=1.0 / GLA_NORMALIZER).then_inc(dk_exp, 1)

                log_part(0)
                for h in range(N_HEADS):
                    if h + 1 < N_HEADS:
                        log_part(h + 1)
                    decay_part(h)
                for h in range(N_HEADS):
                    for j, w in enumerate(LEVELS):
                        act.wait_ge(lv_ready, len(LEVELS) * h + j + 1)
                        lo = 0 if w in S_LEVELS else SAMPLE
                        lv = T((4, 9)[j % 2])[:, lo:TOK]
                        nc.scalar.activation(lv, lv, ACT.Exp, scale=1.0 / GLA_NORMALIZER).then_inc(lv_exp, 1)
                    head_end(h, N_HEADS + h)

            act.wait_ge(norm_in, 16)
            for pp in range(4):
                act.wait_ge(x_in[pp], 16)
                xn_high(0, 2 * pp)
                xn_high(0, 2 * pp + 1)
                squares(0, pp)
                if pp == 0:
                    split(PHASES[0], 0, 0, first=True)
            act.wait_ge(const_in, CONST_ALL)
            nc.scalar.activation(gate_hi[:, :, :], gate_raw[:, :, :], ACT.Copy).then_inc(gate_hi_done, 1)
            act_phases = {"G": g_phase, "D": d_phase, "QK": qk_phase, "V": v_phase, "O": o_phase, "OUT": out_phase}
            for j, ph in enumerate(PHASES):
                if ph["kind"] == "OUT":
                    (mlstm if ph["mixer"] == 0 else gla)()
                act_phases[ph["kind"]](j, ph)
            norm_root(N_NORMS - 1)

        @block.vector
        def _(dve):
            V = nc.vector
            chain = [0]

            def own(ins):
                chain[0] += 1
                ins.then_inc(dve_chain, 1)
                dve.wait_ge(dve_chain, chain[0])

            def split(ph, i, half):
                pair = ph["base"] + 2 * i + half
                for blk in range(2):
                    slot = 2 * half + blk
                    dve.wait_ge(hi_done, 2 * pair + blk + 1)
                    V.tensor_tensor(w_lo[:, slot, :], raw[:, slot, :], w_hi[:, slot, :].bitcast(f32),
                                    ALU.subtract).then_inc(lo_done, 1)

            def split_next(j, i, half):
                ph = PHASES[j]
                if half == 0:
                    split(ph, i, 1)
                elif isinstance(i, int) and 2 * i + 2 == ph["pairs"]:
                    if j + 1 < len(PHASES):
                        split(PHASES[j + 1], 0, 0)
                else:
                    split(ph, i + 1, 0)

            def xn_low(norm, m):
                dve.wait_ge(xn_hi_done, KT_X * norm + m + 1)
                V.scalar_tensor_tensor(xn_lo[:, m, :], x[:, m, :], norm_w[:, norm, m:m + 1],
                                       xn_hi[:, m, :].bitcast(f32), ALU.mult, ALU.subtract).then_inc(xn_ready, 1)

            def add_squares(norm, pp):
                dve.wait_ge(sq_done, 4 * norm + pp + 1)
                if pp:
                    if pp > 1:
                        dve.wait_ge(ssq_done, 3 * norm + pp - 1)
                    V.tensor_tensor(T2(5), T2(5), T2(3), ALU.add).then_inc(ssq_done, 1)

            def norm_rstd(n):
                own(V.tensor_scalar(T(7).rearrange("p (j n) -> p j n", j=3), ps[:, 0:3, HALF_TOK:HALF_TOK + 192],
                                    1.0 / D_MODEL, EPS, ALU.mult, ALU.add))
                V.reciprocal(T(7), T(7)).then_inc(var_ready, 1)
                dve.wait_ge(rstd_ready, n + 1)

            def evac_g(ph, i, half):
                q = ph["hidden"] + 2 * i + half
                m = 2 * i + half
                pair = ph["base"] + 2 * i + half
                b = 4 * half
                V.tensor_tensor(cut2(T(0)), ps[:, b:b + 2, 0:HALF_TOK], cut2(rstd[:, :]), ALU.mult)\
                    .then_inc(tg_ready, 1)
                V.tensor_tensor(cut2(T(1)), ps[:, b + 2:b + 4, 0:HALF_TOK], cut2(rstd[:, :]), ALU.mult)\
                    .then_inc(psum_free, 1)
                dve.wait_ge(psum_free, pair + 1)
                dve.wait_ge(silu_done, q + 1)
                V.tensor_tensor(T(2), T(0), T(1), ALU.mult).then_inc(h_ready, 1)
                dve.wait_ge(hh_done, q + 1)
                hh = h_hi[:, bass.ds(m, 1), :].rearrange("p o t -> p (o t)").bitcast(f32)
                V.tensor_tensor(h_lo[:, bass.ds(m, 1), :].rearrange("p o t -> p (o t)"), T(2), hh, ALU.subtract)\
                    .then_inc(hl_ready, 1)

            def g_phase(j, ph):
                n = ph["pairs"] // 2

                def iteration(i):
                    for half in range(2):
                        split_next(j, i, half)
                        dve.wait_ge(pe_done, ph["base"] + 2 * i + half + 1)
                        if ph["group"] == 0 and half == 0 and i is 0:
                            norm_rstd(ph["norm"])
                        evac_g(ph, i, half)
                iteration(0)
                with dve.Fori(1, n - 1) as i:
                    iteration(i)
                iteration(n - 1)

            def add_to_x(ph, pp, scale, final):
                dve.wait_ge(pe_done, ph["base"] + pp + 1)
                b = 4 * (pp % 2)
                xs = x[:, 2 * pp:2 * pp + 2, :].rearrange("p m (c n) -> p (m c) n", c=2)
                ins = V.scalar_tensor_tensor(xs, ps[:, b:b + 4, 0:HALF_TOK], scale, xs, ALU.mult, ALU.add)
                ins.then_inc(psum_free, 1)
                if final:
                    dve.wait_ge(psum_free, ph["base"] + pp + 1)

            def d_phase(j, ph):
                for pp in range(4):
                    split_next(j, pp // 2, pp % 2)
                    add_to_x(ph, pp, 0.5, final=ph["last"])
                    if ph["last"]:
                        norm = ph["norm"] + 1
                        if norm < N_NORMS - 1:
                            xn_low(norm, 2 * pp)
                            xn_low(norm, 2 * pp + 1)
                        add_squares(norm, pp)

            def out_phase(j, ph):
                norm = ph["norm"] + 1
                for pp in range(4):
                    split_next(j, pp // 2, pp % 2)
                    add_to_x(ph, pp, 1.0, final=True)
                    add_squares(norm, pp)
                for m in range(KT_X):
                    xn_low(norm, m)

            def conv_tile(pair, pp, m):
                b = 4 * (pp % 2) + 2 * (m % 2)
                out = T(m % 2)
                if m >= 2:
                    dve.wait_ge(silu_qk, m - 1)
                if m:
                    dve.wait_ge(conv_ready, m)
                V.tensor_copy(pre_s[:, :, 0:TAIL], conv_in[:, m, :, :])
                V.tensor_tensor(pre_s[:, :, TAIL:], samples(ps[:, b, :]), samples(rstd), ALU.mult)
                V.tensor_tensor(pre_p[:, TAIL:TAIL + HALF_TOK - SAMPLE], ps[:, b, SAMPLE:HALF_TOK],
                                rstd[:, SAMPLE:HALF_TOK], ALU.mult)
                ins = V.tensor_tensor(pre_p[:, TAIL + HALF_TOK - SAMPLE:], ps[:, b + 1, 0:HALF_TOK],
                                      rstd[:, HALF_TOK:], ALU.mult)
                if m % 2:
                    ins.then_inc(psum_free, 1)
                    dve.wait_ge(psum_free, pair + 1)
                else:
                    own(ins)
                V.tensor_copy(conv_out[:, m, 0:1, :], pre_p[:, SEQ:].unsqueeze(1))
                V.tensor_copy(conv_out[:, m, 1:, :], pre_s[:, :, DEC_SEQ:])
                for tap in range(CONV_W):
                    w = conv_w[:, m, tap:tap + 1]
                    src_s, src_p = pre_s[:, :, tap:tap + DEC_SEQ], pre_p[:, tap:tap + SEQ]
                    if tap == 0:
                        bias = conv_w[:, m, CONV_W:CONV_W + 1]
                        V.tensor_scalar(samples(out), src_s, w, bias, ALU.mult, ALU.add)
                        own(V.tensor_scalar(out[:, SAMPLE:], src_p, w, bias, ALU.mult, ALU.add))
                        continue
                    V.scalar_tensor_tensor(samples(out), src_s, w, samples(out), ALU.mult, ALU.add)
                    ins = V.scalar_tensor_tensor(out[:, SAMPLE:], src_p, w, out[:, SAMPLE:], ALU.mult, ALU.add)
                    if tap < CONV_W - 1:
                        own(ins)
                ins.then_inc(conv_ready, 1)

            def qk_phase(j, ph):
                for pp in range(4):
                    split_next(j, pp // 2, pp % 2)
                    dve.wait_ge(pe_done, ph["base"] + pp + 1)
                    if pp == 0:
                        norm_rstd(ph["norm"])
                        if ph["mixer"] == 0:
                            own(V.memset(pre_p[:, 0:TAIL], 0.0))
                    if ph["mixer"] == 0:
                        conv_tile(ph["base"] + pp, pp, 2 * pp)
                        conv_tile(ph["base"] + pp, pp, 2 * pp + 1)
                    else:
                        for blk in range(2):
                            m, b = 2 * pp + blk, 4 * (pp % 2) + 2 * blk
                            dst = qt[:, m, :] if m < N_HEADS else kt[:, m - N_HEADS, :]
                            scale = QK_SCALE if m < N_HEADS else 1.0
                            ins = V.scalar_tensor_tensor(cut2(dst), ps[:, b:b + 2, 0:HALF_TOK], scale,
                                                         cut2(rstd[:, :]), ALU.mult, ALU.mult)
                        ins.then_inc(psum_free, 1)
                if ph["mixer"] == 0:
                    dve.wait_ge(silu_qk, KT_X)
                    V.tensor_scalar(kt[:, :, :], kt[:, :, :], QK_SCALE, None, ALU.mult).then_inc(k_scaled, 1)

            def v_phase(j, ph):
                for pp in range(4):
                    split_next(j, pp // 2, pp % 2)
                    dve.wait_ge(pe_done, ph["base"] + pp + 1)
                    if pp == 0:
                        own(V.tensor_copy(rstd_tok[:, :], ps[:, 3, 0:TT]))
                    b = 4 * (pp % 2)
                    src = ps[:, b:b + 3, :].rearrange("p a n -> p (a n)")[:, 0:TT * 256]\
                        .rearrange("p (t n) -> p t n", n=256)
                    V.tensor_tensor(v_tok[:, :, pp * 256:(pp + 1) * 256], src, bcast(rstd_tok[:, :], 256),
                                    ALU.mult).then_inc(psum_free, 1)

            def o_phase(j, ph):
                for pp in range(4):
                    split_next(j, pp // 2, pp % 2)
                    dve.wait_ge(pe_done, ph["base"] + pp + 1)
                    b = 4 * (pp % 2)
                    for blk in range(2):
                        ins = V.tensor_tensor(cut2(og[:, 2 * pp + blk, :]), ps[:, b + 2 * blk:b + 2 * blk + 2, 0:HALF_TOK],
                                              cut2(rstd[:, :]), ALU.mult)
                    ins.then_inc(psum_free, 1)

            def gates_token_major(mixer):
                n = 2 * N_HEADS if mixer == 0 else GATE_RANK
                dve.wait_ge(gates_done, mixer + 1)
                src = ps[:, 0, 0:TT * GATE_RANK].rearrange("p (t n) -> p t n", n=GATE_RANK)[:, :, 0:n]
                V.tensor_tensor(gate_tok[:, :, 0:n], src, bcast(rstd_tok[:, :], n), ALU.mult)\
                    .then_inc(gate_tok_ready, 1)

            def log_sigmoid_in(z, t):
                return V.scalar_tensor_tensor(t, z, -1.0, z, ALU.mult, ALU.min)

            def log_sigmoid_out(out, z, t):
                return V.scalar_tensor_tensor(out, z, 0.0, t, ALU.min, ALU.subtract)

            def mlstm_gates():
                R = slice(0, N_HEADS)
                ig, z, t2, d0, big_m, m_prev, tmp, sc = (T(i)[R] for i in range(8))
                dve.wait_ge(rows_done, 1)
                for dst, bank, col, bias in ((ig, 1, 0, 0), (z, 2, SAMPLE, 1)):
                    V.tensor_scalar(dst[:, SAMPLE:], ps[R, bank, :], gate_bias[:, bias:bias + 1], None, ALU.add)
                    own(V.tensor_scalar(dst[:, 0:SAMPLE], ps[R, 3, col:col + SAMPLE], gate_bias[:, bias:bias + 1],
                                        None, ALU.add))
                log_sigmoid_in(z, t2).then_inc(rz_ready, 1)
                dve.wait_ge(rz_exp, 1)
                own(log_sigmoid_out(z, z, t2))
                b, g = t2, z
                own(V.tensor_tensor_scan(b, reset[R], z, 0.0, ALU.mult, ALU.add))
                own(V.tensor_tensor(g, ig, b, ALU.subtract))
                own(V.tensor_copy(d0[:, 0:SAMPLE], g[:, 0:SAMPLE]))
                own(V.tensor_tensor(samples(d0)[:, :, 0], samples(g)[:, :, 0], m_in[:, :], ALU.max))
                own(V.memset(d0[:, SAMPLE:], 0.0))
                own(V.tensor_copy(chunks(d0)[:, 1:, 0], chunks(b)[:, 0:N_CH - 1, P - 1]))
                V.tensor_tensor_scan(big_m[:, 0:SAMPLE], drop, d0[:, 0:SAMPLE], NEG, ALU.add, ALU.max)
                own(V.tensor_tensor_scan(big_m[:, SAMPLE:], d0[:, SAMPLE:], g[:, SAMPLE:], 0.0, ALU.add, ALU.max))
                own(V.tensor_tensor(tmp[:, 0:N_CH], chunks(big_m)[:, :, P - 1], chunks(b)[:, :, P - 1], ALU.add))
                V.tensor_copy(m_out[:, 0:1], tmp[:, N_CH - 1:N_CH])
                V.tensor_tensor(m_out[:, 1:], samples(big_m)[:, :, DEC_SEQ - 1], samples(b)[:, :, DEC_SEQ - 1],
                                ALU.add)
                V.tensor_copy(samples(m_prev), bcast(m_in[:, :], DEC_SEQ))
                V.memset(m_prev[:, SAMPLE:SAMPLE + P], 0.0)
                own(V.tensor_copy(chunks(m_prev)[:, 1:, :], bcast(tmp[:, 0:N_CH - 1], P)))
                V.tensor_scalar(rows[R, 0, :], big_m, -1.0, None, ALU.mult)
                V.tensor_tensor(rows[R, 1, :], m_prev, big_m, ALU.subtract)
                V.scalar_tensor_tensor(rows[R, 2, :], b, -1.0, big_m, ALU.mult, ALU.subtract)
                for part, n in ((samples, DEC_SEQ), (chunks, P)):
                    ins = V.tensor_tensor(part(sc), part(g), bcast(part(big_m)[:, :, n - 1], n), ALU.subtract)
                ins.then_inc(rexp_ready, 1)
                dve.wait_ge(cols_done, 1)
                src = ps[:, 3, 256:256 + 8 * TT].rearrange("p (t n) -> p t n", n=8)
                V.tensor_copy(cols[0:SAMPLE, 0, :], src[0:SAMPLE, 0, :])
                V.tensor_copy(cols[:, 1:, :], src[:, 1:, :]).then_inc(cols_ready, 1)
                dve.wait_ge(cols_ready, 1)

            def gla_gates():
                dve.wait_ge(rows_done, 2)
                V.tensor_copy(rows[0:GATE_RANK, 0, 0:SAMPLE], ps[0:GATE_RANK, 2, 0:SAMPLE])
                V.tensor_copy(rows[0:GATE_RANK, 0, SAMPLE:], ps[0:GATE_RANK, 1, :]).then_inc(cols_ready, 1)

                def log_sigmoid_start(h):
                    dve.wait_ge(bc_done, N_HEADS + h + 1)
                    for j, (a, b) in enumerate(PIECES):
                        ins = V.tensor_scalar(zz(h)[:, a:b], ps[:, 2 * h + j, 0:b - a], b_a[:, h:h + 1], None, ALU.add)
                    own(ins)
                    log_sigmoid_in(zz(h), kb(h)).then_inc(e_ready, 1)

                def cumulate(h):
                    dve.wait_ge(e_exp, N_HEADS + h + 1)
                    own(log_sigmoid_out(zz(h), zz(h), kb(h)))
                    V.tensor_tensor_scan(bb(h), reset, zz(h), 0.0, ALU.mult, ALU.add).then_inc(b_ready, 1)
                    dve.wait_ge(b_ready, h + 1)
                    V.tensor_tensor(samples(kb(h)), bcast(samples(bb(h))[:, :, DEC_SEQ - 1], DEC_SEQ), samples(bb(h)),
                                    ALU.subtract)
                    V.tensor_tensor(chunks(kb(h)), bcast(chunks(bb(h))[:, :, P - 1], P), chunks(bb(h)), ALU.subtract)\
                        .then_inc(dk_ready, 1)

                def apply_decay(h):
                    dve.wait_ge(eb_done, h + 1)
                    V.tensor_copy(decays[:, h, 0:DEC_BATCH], samples(qb(h))[:, :, DEC_SEQ - 1])
                    own(V.tensor_copy(decays[:, h, DEC_BATCH:], chunks(qb(h))[:, :, P - 1]))
                    V.tensor_tensor(qb(h), qb(h), qt[:, h, :], ALU.mult)
                    dve.wait_ge(dk_exp, h + 1)
                    V.tensor_tensor(kb(h), kb(h), kt[:, h, :], ALU.mult).then_inc(kb_ready, 1)

                log_sigmoid_start(0)
                for h in range(N_HEADS):
                    if h + 1 < N_HEADS:
                        log_sigmoid_start(h + 1)
                    if h:
                        apply_decay(h - 1)
                    cumulate(h)
                apply_decay(N_HEADS - 1)

            def sample_keys():
                return V.tensor_tensor(k_tok_b[:, :, :], bcast_mid(k_tok_s[:, :], DEC_BATCH), bcast(batch, DK),
                                       ALU.mult)

            def prompt_states(h):
                for c in range(N_CH):
                    upd = ps[:, c // 2, (c % 2) * DV:(c % 2 + 1) * DV]
                    if c == 0:
                        ins = V.tensor_copy(state[:, 0, :], upd)
                    else:
                        ins = V.scalar_tensor_tensor(state[:, c, :], state[:, c - 1, :],
                                                     decays[:, h, DEC_BATCH + c:DEC_BATCH + c + 1], upd,
                                                     ALU.mult, ALU.add)
                    if c < N_CH - 1:
                        own(ins)
                return ins

            def sample_states(h, u):
                dve.wait_ge(us_done, u + 1)
                for b in range(DEC_BATCH):
                    upd = ps[:, (3, 5, 6, 7)[b // 2], (b % 2) * DV:(b % 2 + 1) * DV]
                    ins = V.scalar_tensor_tensor(state_s[:, b, :], state_s[:, b, :], decays[:, h, b:b + 1], upd,
                                                 ALU.mult, ALU.add)
                ins.then_inc(state_ready, 1)

            def head_end(h, u, den):
                sample_states(h, u)
                dve.wait_ge(hsum_done, u + 1)
                for (a, b), bank in zip(PIECES, (2, 4)):
                    src = ps[:, bank, 0:b - a]
                    if den:
                        ins = V.scalar_tensor_tensor(T(9)[:, a:b], src, 1.0 / DV, T(2)[:, a:b], ALU.mult, ALU.add)
                    else:
                        ins = V.tensor_scalar(T(9)[:, a:b], src, 1.0 / DV, EPS, ALU.mult, ALU.add)
                ins.then_inc(hvar_ready, 1)
                dve.wait_ge(hr_ready, u + 1)
                for a in range(2):
                    m = 2 * h + a
                    own(V.scalar_tensor_tensor(T(7 + a), T(7 + a), head_w[:, u // N_HEADS, m:m + 1], T(9),
                                               ALU.mult, ALU.mult))
                dve.wait_ge(og_done, 4 * (u // N_HEADS + 1))
                V.tensor_tensor(T2(7), T2(7), og[:, 2 * h:2 * h + 2, :], ALU.mult).then_inc(y_ready, 1)
                dve.wait_ge(y_hi, u + 1)
                V.tensor_tensor(xn_lo[:, 2 * h:2 * h + 2, :], T2(7), xn_hi[:, 2 * h:2 * h + 2, :].bitcast(f32),
                                ALU.subtract).then_inc(y_lo, 1)

            def take_output(u):
                dve.wait_ge(num_done, u + 1)
                for d in range(2):
                    for j, (a, b) in enumerate(PIECES):
                        ins = V.tensor_copy(T(7 + d)[:, a:b], ps[:, ((3, 5), (6, 7))[d][j], 0:b - a])
                ins.then_inc(ht_ready, 1)

            def mlstm_head(h):
                u = h
                if h:
                    dve.wait_ge(state_out, 32 * u)
                dve.wait_ge(bc_done, u + 1)
                g_col = cols[:, :, h]
                V.scalar_tensor_tensor(att_s(3), ps[0:SAMPLE, 0, 0:SAMPLE], g_col[0:SAMPLE, 0:1], causal_s,
                                       ALU.add, ALU.add)
                for c in range(N_CH):
                    at = TILE_AT[1 + c] - PIECES[c // 2][0]
                    ins = V.scalar_tensor_tensor(T(3)[:, c * P:(c + 1) * P], ps[:, c // 2, at:at + P],
                                                 g_col[:, 1 + c:2 + c], causal, ALU.add, ALU.add)
                ins.then_inc(e_ready, 1)
                V.tensor_copy(decays[:, h, 0:DEC_BATCH], samples(ps[:, 2, :])[:, :, DEC_SEQ - 1])
                for j in range(2):
                    ends = [TILE_AT[1 + c] + P - 1 - PIECES[j][0] for c in (2 * j, 2 * j + 1)]
                    V.tensor_copy(decays[:, h, DEC_BATCH + 2 * j:DEC_BATCH + 2 * j + 2],
                                  ps[:, 2 + j, ends[0]:ends[1] + 1:P])
                V.tensor_tensor(T(0)[:, 0:CUT], qt[:, h, 0:CUT], ps[:, 2, 0:CUT], ALU.mult)
                V.tensor_tensor(T(0)[:, CUT:], qt[:, h, CUT:], ps[:, 3, 0:TOK - CUT], ALU.mult).then_inc(qw_ready, 1)
                dve.wait_ge(qw_ready, u + 1)
                dve.wait_ge(ktok_done, u + 1)
                sc = cols[:, :, N_HEADS + h]
                own(V.tensor_scalar(k_tok_s[:, :], ps[0:SAMPLE, 7, 0:DK], sc[0:SAMPLE, 0:1], None, ALU.mult))
                V.tensor_tensor(k_tok[:, :, :], ps[:, 6, :].rearrange("p (c n) -> p c n", n=DK), bcast(sc[:, 1:], DK),
                                ALU.mult)
                sample_keys().then_inc(ktok_ready, 1)
                dve.wait_ge(e_exp, u + 1)
                dve.wait_ge(scores_done, u + 1)
                V.tensor_tensor(att_s(4), att_s(3), ps[0:SAMPLE, 5, 0:SAMPLE], ALU.mult)
                V.tensor_tensor(T(4)[:, 0:SEQ], T(3)[:, 0:SEQ], ps[:, 4, :], ALU.mult).then_inc(att_ready, 1)
                dve.wait_ge(u_done, u + 1)
                prompt_states(h)
                for c in range(N_CH):
                    upd = ps[:, 2, 448 + c:449 + c]
                    if c == 0:
                        own(V.tensor_copy(n_state[:, 0:1], upd))
                    else:
                        own(V.scalar_tensor_tensor(n_state[:, c:c + 1], n_state[:, c - 1:c],
                                                   decays[:, h, DEC_BATCH + c:DEC_BATCH + c + 1], upd,
                                                   ALU.mult, ALU.add))
                V.tensor_copy(n_out[:, h, 0:1], n_state[:, N_CH - 1:N_CH])
                own(V.tensor_tensor(n_out[:, h, 1:], n_in[:, h, :], decays[:, h, 0:DEC_BATCH], ALU.mult))
                V.tensor_tensor(n_out[:, h, 1:], n_out[:, h, 1:], ps[:, 2, 456:456 + DEC_BATCH], ALU.add)\
                    .then_inc(states_ready, 1)
                V.tensor_tensor(samples(T(1)), samples(T(0)), bcast(n_in[:, h, :], DEC_SEQ), ALU.mult)
                for c in range(1, N_CH):
                    ts = slice(TILE_AT[1 + c], TILE_AT[1 + c] + P)
                    ins = V.tensor_scalar(T(1)[:, ts], T(0)[:, ts], n_state[:, c - 1:c], None, ALU.mult)
                ins.then_inc(qn_ready, 1)
                take_output(u)
                dve.wait_ge(den_abs, u + 1)
                for j, (a, b) in enumerate(PIECES):
                    own(V.tensor_tensor(T(2)[:, a:b], T(2)[:, a:b], ps[:, j, 0:b - a], ALU.max))
                own(V.tensor_scalar(T(2), T(2), D_MAX, None, ALU.min))
                own(V.scalar_tensor_tensor(T(2), T(2), EPS, T(2), ALU.mult, ALU.mult))
                head_end(h, u, True)

            def gla_head(h):
                u = N_HEADS + h
                dve.wait_ge(state_out, 32 * u)
                bv_all, q, k = bb(h), qt[:, h, :], kt[:, h, :]

                def level_exponents(j):
                    w = LEVELS[j]
                    lo = 0 if w in S_LEVELS else SAMPLE
                    lv = T((4, 9)[j % 2])[:, lo:].rearrange("p (n w) -> p n w", w=2 * w)
                    bv = bv_all[:, lo:].rearrange("p (n w) -> p n w", w=2 * w)
                    ref = bcast(bv[:, :, w - 1], w)
                    V.tensor_tensor(lv[:, :, 0:w], ref, bv[:, :, 0:w], ALU.subtract)
                    V.tensor_tensor(lv[:, :, w:], bv[:, :, w:], ref, ALU.subtract).then_inc(lv_ready, 1)

                def level_operands(j):
                    dve.wait_ge(lv_exp, len(LEVELS) * h + j + 1)
                    if j >= 2:
                        dve.wait_ge(lvl_done, len(LEVELS) * h + j - 1)
                    w = LEVELS[j]
                    lo = 0 if w in S_LEVELS else SAMPLE
                    lv, ke, qe, kv, qv = (a[:, lo:].rearrange("p (n w) -> p n w", w=2 * w)
                                          for a in (T((4, 9)[j % 2]), T(5 + 2 * (j % 2)), T(6 + 2 * (j % 2)), k, q))
                    V.tensor_tensor(ke[:, :, 0:w], kv[:, :, 0:w], lv[:, :, 0:w], ALU.mult)
                    V.tensor_tensor(qe[:, :, w:], qv[:, :, w:], lv[:, :, w:], ALU.mult).then_inc(lq_ready, 1)

                def level_take(j):
                    dve.wait_ge(lvl_done, len(LEVELS) * h + j + 1)
                    w = LEVELS[j]
                    if w in S_LEVELS:
                        own(V.copy_predicated(att_s(2), level_mask[0:SAMPLE, j + 1, 0:SAMPLE],
                                              ps[0:SAMPLE, (4, 0)[j % 2], 0:SAMPLE]))
                    ins = V.copy_predicated(T(2)[:, 0:SEQ].rearrange("p (c n) -> p c n", n=P),
                                            bcast_mid(level_mask[:, j + 1, :], N_CH),
                                            ps[:, 2 + j % 2, :].rearrange("p (c n) -> p c n", n=P))
                    if j == len(LEVELS) - 1:
                        ins.then_inc(att_ready, 1)
                    else:
                        own(ins)

                if h == 0:
                    V.memset(scratch[:, 5:9, :], 0.0)
                level_exponents(0)
                dve.wait_ge(scores_done, u + 1)
                V.tensor_tensor(att_s(2), ps[0:SAMPLE, 4, 0:SAMPLE], ident[0:SAMPLE, 0:SAMPLE], ALU.mult)
                own(V.tensor_tensor(T(2)[:, 0:SEQ].rearrange("p (c n) -> p c n", n=P),
                                    ps[:, 5, :].rearrange("p (c n) -> p c n", n=P), bcast_mid(ident, N_CH), ALU.mult))
                level_exponents(1)
                dve.wait_ge(ktok_done, u + 1)
                own(V.tensor_copy(k_tok_s[:, :], ps[0:SAMPLE, 7, 0:DK]))
                V.tensor_copy(k_tok[:, :, :], ps[:, 6, :].rearrange("p (c n) -> p c n", n=DK))
                sample_keys().then_inc(ktok_ready, 1)
                level_operands(0)
                dve.wait_ge(u_done, u + 1)
                prompt_states(h).then_inc(states_ready, 1)
                for j in range(1, len(LEVELS)):
                    level_operands(j)
                    if j + 1 < len(LEVELS):
                        level_exponents(j + 1)
                    level_take(j - 1)
                level_take(len(LEVELS) - 1)
                take_output(u)
                head_end(h, u, False)

            for pp in range(4):
                xn_low(0, 2 * pp)
                xn_low(0, 2 * pp + 1)
                add_squares(0, pp)
                if pp == 0:
                    split(PHASES[0], 0, 0)
            dve.wait_ge(const_in, CONST_ALL)
            V.tensor_copy(level_mask[:, :, :].rearrange("p l n -> p (l n)"), v_tok[:, 0, :])
            dve.wait_ge(gate_hi_done, 1)
            V.tensor_tensor(gate_lo[:, :, :], gate_raw[:, :, :], gate_hi[:, :, :].bitcast(f32), ALU.subtract)\
                .then_inc(gate_lo_done, 1)
            dve_phases = {"G": g_phase, "D": d_phase, "QK": qk_phase, "V": v_phase, "O": o_phase, "OUT": out_phase}
            for j, ph in enumerate(PHASES):
                if ph["kind"] == "OUT":
                    gates_token_major(ph["mixer"])
                    (mlstm_gates if ph["mixer"] == 0 else gla_gates)()
                    for h in range(N_HEADS):
                        (mlstm_head if ph["mixer"] == 0 else gla_head)(h)
                dve_phases[ph["kind"]](j, ph)
            dve.wait_ge(pe_done, N_PAIRS + 1)
            norm_rstd(N_NORMS - 1)
            for m in range(KT_X):
                V.scalar_tensor_tensor(x[:, m, :], x[:, m, :], norm_w[:, N_NORMS - 1, m:m + 1], rstd[:, :],
                                       ALU.mult, ALU.mult).then_inc(final_ready, 1)


def kernel(**inputs):
    import concourse.bacc as bacc
    from concourse.bass_utils import run_bass_kernel_spmd

    a = {k: np.asarray(v) for k, v in inputs.items()}
    table, level = constants()

    def tiles(w):
        w = w.reshape(-1, w.shape[-2] // P, P, w.shape[-1] // P, P)
        return w.transpose(0, 3, 2, 1, 4).reshape(-1, P, w.shape[1] * P)

    def by_feature(v):
        v = v.reshape(v.shape[:-1] + (-1, P))
        return np.moveaxis(v, -1, 0)

    w0, w1 = a["mlstm_w_in"][0], a["gla_w_in"][0]
    wide = 2 * N_HEADS * DK + 2 * N_HEADS * DV
    tokens = np.concatenate([a["x_sample"].reshape(SAMPLE, D_MODEL), a["x_prompt"].reshape(SEQ, D_MODEL)])
    arrays = {
        "x": by_feature(tokens).transpose(0, 2, 1),
        "w_gate": tiles(a["ffn_w_gate"]), "w_up": tiles(a["ffn_w_up"]), "w_down": tiles(a["ffn_w_down"]),
        "w_mix": np.concatenate([tiles(w0[:, :wide]), tiles(a["mlstm_w_out"]),
                                 tiles(w1[:, :wide]), tiles(a["gla_w_out"])]),
        "state_c": a["state_mlstm_C"][0], "state_g": a["state_gla_S"][0],
    }
    norms = np.concatenate([a["norm_w"].reshape(6, D_MODEL), a["final_norm_w"][None]])
    small = {
        "norm_w": by_feature(norms),
        "table": table, "level": level,
        "head_w": by_feature(np.concatenate([a["mlstm_hnorm_w"], a["gla_hnorm_w"]])),
        "conv_w": by_feature(np.concatenate([a["mlstm_conv_w"][0], a["mlstm_conv_b"]])).transpose(0, 2, 1),
        "conv_in": by_feature(a["state_mlstm_conv"][0]).transpose(0, 3, 1, 2),
        "gates0": w0[:, wide:].reshape(KT_X, P, -1).transpose(1, 0, 2),
        "gates1": w1[:, wide:].reshape(KT_X, P, -1).transpose(1, 0, 2),
        "gate_bias": np.stack([a["mlstm_b_i"][0], a["mlstm_b_f"][0]], 1),
        "m_in": a["state_mlstm_m"][0].T,
        "w_a2": a["gla_w_a2"][0],
        "b_a": by_feature(a["gla_b_a"][0]),
        "n_in": a["state_mlstm_n"][0].transpose(2, 1, 0),
    }
    outs = {
        "y": (P, KT_X, TOK), "c_p": (N_HEADS, DK, DV), "s_p": (N_HEADS, DK, DV),
        "c_s": (DEC_BATCH, N_HEADS, DK, DV), "s_s": (DEC_BATCH, N_HEADS, DK, DV),
        "n_out": (P, N_HEADS, DEC_BATCH + 1), "m_out": (N_HEADS, DEC_BATCH + 1),
        "conv_out": (P, KT_X, DEC_BATCH + 1, TAIL),
    }
    nc = bacc.Bacc("TRN2", target_bir_lowering=False, num_devices=1, dynamic_dma_scratch_size=1024)
    io, feed = {"small": []}, {}
    for group in (arrays, small):
        for name, v in group.items():
            v = np.ascontiguousarray(v)
            feed["in_" + name] = v
            ap = nc.dram_tensor("in_" + name, v.shape, mybir.dt.from_np(v.dtype), kind="ExternalInput").ap()
            if group is small:
                io["small"].append(ap)
            else:
                io[name] = ap
    for name, shape in outs.items():
        io[name] = nc.dram_tensor("out_" + name, shape, mybir.dt.float32, kind="ExternalOutput").ap()
    program(nc, io)
    r = run_bass_kernel_spmd(nc, [feed], core_ids=[0]).results[0]
    o = {name: r["out_" + name] for name in outs}

    y = o["y"].transpose(2, 1, 0).reshape(TOK, D_MODEL)
    n = o["n_out"].transpose(2, 1, 0)
    m = o["m_out"].T
    conv = o["conv_out"].transpose(2, 3, 1, 0).reshape(DEC_BATCH + 1, TAIL, D_MODEL)
    return (y[SAMPLE:].reshape(1, SEQ, D_MODEL), y[:SAMPLE].reshape(DEC_BATCH, DEC_SEQ, D_MODEL),
            o["c_p"][None, None], n[None, 0:1], m[None, 0:1], conv[None, 0:1], o["s_p"][None, None],
            o["c_s"][None], n[None, 1:], m[None, 1:], conv[None, 1:], o["s_s"][None])
```
